# Optimizing a Trainium2 kernel written in Bass

```python
import jax, jax.numpy as jnp
from jax import lax
import numpy as np

D_MODEL = 1024
BATCH = 1
SEQ = 128
DEPTH = 2
DEC_BATCH = 1
DEC_SEQ = 512
PAST_LEN = 128

GRID_W = 64
N_MIXERS = 2
N_DA = (DEPTH + 1) // 2
N_MLA = DEPTH // 2
DA_HEADS = 8
DA_HEAD_DIM = 64
DA_V_DIM = 2 * DA_HEAD_DIM
MLA_HEADS = 16
MLA_Q_LORA = 512
MLA_KV_LORA = 256
MLA_NOPE = 64
MLA_ROPE = 32
MLA_QK_DIM = MLA_NOPE + MLA_ROPE
MLA_V_DIM = 64
PEER_HEADS = 8
PEER_N_KEYS = 128
PEER_N_EXPERTS = PEER_N_KEYS * PEER_N_KEYS
PEER_KEY_DIM = 256
PEER_HALF = PEER_KEY_DIM // 2
PEER_TOPK = 16
Q_BLOCK = 128
TOK_BLOCK = 128
ROPE_BASE = 10000.0
EPS = 1e-6

kernel_name = "hybrid_diffattn_mla_peer_prefix_dit_step"

def rms_norm(x, g):
    xf = x.astype(jnp.float32)
    y = xf * lax.rsqrt(jnp.mean(xf * xf, axis=-1, keepdims=True) + EPS)
    return (y * g.astype(jnp.float32)).astype(x.dtype)

def rope_1d(x, pos):
    d = x.shape[-1]
    inv = 1.0 / (ROPE_BASE ** (jnp.arange(0, d, 2, dtype=jnp.float32) / d))
    ang = pos[:, None] * inv[None, :]
    cos = jnp.cos(ang)[None, :, None, :]
    sin = jnp.sin(ang)[None, :, None, :]
    xf = x.astype(jnp.float32)
    x1, x2 = xf[..., : d // 2], xf[..., d // 2:]
    return jnp.concatenate([x1 * cos - x2 * sin, x2 * cos + x1 * sin], axis=-1).astype(x.dtype)

def rope_2d(x, row, col):
    h = x.shape[-1] // 2
    return jnp.concatenate([rope_1d(x[..., :h], row), rope_1d(x[..., h:], col)], axis=-1)

def grid_positions(n):
    rows = n // GRID_W
    row = jnp.repeat(jnp.arange(rows, dtype=jnp.float32), GRID_W)
    col = jnp.tile(jnp.arange(GRID_W, dtype=jnp.float32), rows)
    return row, col

def modulation(cvec, w, b):
    m = jax.nn.silu(cvec) @ w + b
    return [t[:, None, :] for t in jnp.split(m, 6, axis=-1)]

def modulate(x, g, shift, scale):
    return rms_norm(x, g) * (1.0 + scale) + shift

def attend(q, k, v, mix):
    B, S, Hq, Dq = q.shape
    scale = Dq ** -0.5
    nb = S // Q_BLOCK
    qb = q.reshape(B, nb, Q_BLOCK, Hq, Dq).swapaxes(0, 1)

    def one(qblk):
        s = jnp.einsum('bqhd,bkhd->bhqk', qblk, k, preferred_element_type=jnp.float32) * scale
        w = mix(jax.nn.softmax(s, axis=-1))
        return jnp.einsum('bhqk,bkhd->bqhd', w.astype(v.dtype), v)

    o = lax.map(one, qb)
    return o.swapaxes(0, 1).reshape(B, S, o.shape[-2], o.shape[-1])

def da_qkv(h, wq, wk, wv, qn, kn, pos):
    B, S, _ = h.shape
    q = rms_norm((h @ wq).reshape(B, S, 2 * DA_HEADS, DA_HEAD_DIM), qn)
    k = rms_norm((h @ wk).reshape(B, S, 2 * DA_HEADS, DA_HEAD_DIM), kn)
    v = (h @ wv).reshape(B, S, DA_HEADS, DA_V_DIM)
    if pos is not None:
        q = rope_2d(q, pos[0], pos[1])
        k = rope_2d(k, pos[0], pos[1])
    return q, k, v

def da_out(q, k, v, lam, lam_init, subln, wo):
    def mix(p):
        b, h2, nq, nk = p.shape
        p = p.reshape(b, h2 // 2, 2, nq, nk)
        return p[:, :, 0] - lam * p[:, :, 1]

    o = attend(q, k, v, mix)
    o = rms_norm(o, subln) * (1.0 - lam_init)
    B, S = o.shape[:2]
    return o.reshape(B, S, DA_HEADS * DA_V_DIM) @ wo

def mla_query(h, wdq, qa_norm, wuq, q_norm, pos):
    B, S, _ = h.shape
    q = (rms_norm(h @ wdq, qa_norm) @ wuq).reshape(B, S, MLA_HEADS, MLA_QK_DIM)
    q = rms_norm(q, q_norm)
    if pos is not None:
        q = jnp.concatenate([q[..., :MLA_NOPE], rope_2d(q[..., MLA_NOPE:], pos[0], pos[1])], axis=-1)
    return q

def mla_compress(h, wdkv, kv_norm):
    ckv = h @ wdkv
    return rms_norm(ckv[..., :MLA_KV_LORA], kv_norm), ckv[..., MLA_KV_LORA:]

def mla_expand(ckv, kpe, wukv, k_norm, pos):
    B, S, _ = ckv.shape
    kv = (ckv @ wukv).reshape(B, S, MLA_HEADS, MLA_NOPE + MLA_V_DIM)
    k_nope, v = kv[..., :MLA_NOPE], kv[..., MLA_NOPE:]
    k_pe = jnp.broadcast_to(kpe[:, :, None, :], (B, S, MLA_HEADS, MLA_ROPE))
    k = rms_norm(jnp.concatenate([k_nope, k_pe], axis=-1), k_norm)
    if pos is not None:
        k = jnp.concatenate([k[..., :MLA_NOPE], rope_2d(k[..., MLA_NOPE:], pos[0], pos[1])], axis=-1)
    return k, v

def mla_out(q, k, v, wo):
    o = attend(q, k, v, lambda p: p)
    B, S = o.shape[:2]
    return o.reshape(B, S, MLA_HEADS * MLA_V_DIM) @ wo

def peer(h, wq, sub_keys, u, v):
    B, S, D = h.shape
    xb_all = h.reshape((B * S) // TOK_BLOCK, TOK_BLOCK, D)

    def one(xb):
        q = (xb @ wq).reshape(TOK_BLOCK, PEER_HEADS, 2, PEER_HALF)
        s = jnp.einsum('thcd,hcnd->thcn', q, sub_keys, preferred_element_type=jnp.float32)
        top_s, top_i = lax.top_k(s, PEER_TOPK)
        cand_s = top_s[:, :, 0, :, None] + top_s[:, :, 1, None, :]
        cand_i = top_i[:, :, 0, :, None] * PEER_N_KEYS + top_i[:, :, 1, None, :]
        cand_s = cand_s.reshape(TOK_BLOCK, PEER_HEADS, PEER_TOPK * PEER_TOPK)
        cand_i = cand_i.reshape(TOK_BLOCK, PEER_HEADS, PEER_TOPK * PEER_TOPK)
        fs, fi = lax.top_k(cand_s, PEER_TOPK)
        idx = jnp.take_along_axis(cand_i, fi, axis=-1)
        g = jax.nn.softmax(fs, axis=-1)
        ue = u[idx]
        a = jax.nn.gelu(jnp.einsum('td,thkd->thk', xb, ue, preferred_element_type=jnp.float32))
        ve = v[idx]
        return jnp.einsum('thk,thkd->td', (g * a).astype(xb.dtype), ve)

    return lax.map(one, xb_all).reshape(B, S, D)

def setup_inputs(seed: int = 0) -> dict:
    key = jax.random.key(seed)
    ks = iter(jax.random.split(key, 64))

    def nrm(shape, scale=1.0):
        return jax.random.normal(next(ks), shape, jnp.float32) * scale

    def gain(shape):
        return 1.0 + nrm(shape, 0.02)

    D = D_MODEL
    fan = D ** -0.5
    return {
        "x_prompt": nrm((BATCH, SEQ, D)),
        "x_sample": nrm((DEC_BATCH, DEC_SEQ, D)),
        "cache_da_k": nrm((DEC_BATCH, N_DA, PAST_LEN, 2 * DA_HEADS, DA_HEAD_DIM)),
        "cache_da_v": nrm((DEC_BATCH, N_DA, PAST_LEN, DA_HEADS, DA_V_DIM)),
        "cache_mla_ckv": nrm((DEC_BATCH, N_MLA, PAST_LEN, MLA_KV_LORA)),
        "cache_mla_kpe": nrm((DEC_BATCH, N_MLA, PAST_LEN, MLA_ROPE)),
        "c": nrm((DEC_BATCH, D)),
        "c_ctx": nrm((D,)),
        "norm1": gain((DEPTH, D)),
        "norm2": gain((DEPTH, D)),
        "ada_w": nrm((DEPTH, D, 6 * D), 0.5 * fan),
        "ada_b": nrm((DEPTH, 6 * D), 0.02),
        "da_wq": nrm((N_DA, D, 2 * DA_HEADS * DA_HEAD_DIM), fan),
        "da_wk": nrm((N_DA, D, 2 * DA_HEADS * DA_HEAD_DIM), fan),
        "da_wv": nrm((N_DA, D, DA_HEADS * DA_V_DIM), fan),
        "da_wo": nrm((N_DA, DA_HEADS * DA_V_DIM, D), (DA_HEADS * DA_V_DIM) ** -0.5),
        "da_q_norm": gain((N_DA, DA_HEAD_DIM)),
        "da_k_norm": gain((N_DA, DA_HEAD_DIM)),
        "da_lq1": nrm((N_DA, DA_HEAD_DIM), 0.1),
        "da_lk1": nrm((N_DA, DA_HEAD_DIM), 0.1),
        "da_lq2": nrm((N_DA, DA_HEAD_DIM), 0.1),
        "da_lk2": nrm((N_DA, DA_HEAD_DIM), 0.1),
        "da_subln": gain((N_DA, DA_V_DIM)),
        "mla_wdq": nrm((N_MLA, D, MLA_Q_LORA), fan),
        "mla_qa_norm": gain((N_MLA, MLA_Q_LORA)),
        "mla_wuq": nrm((N_MLA, MLA_Q_LORA, MLA_HEADS * MLA_QK_DIM), MLA_Q_LORA ** -0.5),
        "mla_wdkv": nrm((N_MLA, D, MLA_KV_LORA + MLA_ROPE), fan),
        "mla_kv_norm": gain((N_MLA, MLA_KV_LORA)),
        "mla_wukv": nrm((N_MLA, MLA_KV_LORA, MLA_HEADS * (MLA_NOPE + MLA_V_DIM)), MLA_KV_LORA ** -0.5),
        "mla_q_norm": gain((N_MLA, MLA_QK_DIM)),
        "mla_k_norm": gain((N_MLA, MLA_QK_DIM)),
        "mla_wo": nrm((N_MLA, MLA_HEADS * MLA_V_DIM, D), (MLA_HEADS * MLA_V_DIM) ** -0.5),
        "peer_wq": nrm((DEPTH, D, PEER_HEADS * PEER_KEY_DIM), fan),
        "peer_keys": nrm((DEPTH, PEER_HEADS, 2, PEER_N_KEYS, PEER_HALF), PEER_HALF ** -0.5),
        "peer_u": nrm((DEPTH, PEER_N_EXPERTS, D), fan),
        "peer_v": nrm((DEPTH, PEER_N_EXPERTS, D), 0.5),
    }

def reference(x_prompt, x_sample, cache_da_k, cache_da_v, cache_mla_ckv, cache_mla_kpe, c, c_ctx,
              norm1, norm2, ada_w, ada_b,
              da_wq, da_wk, da_wv, da_wo, da_q_norm, da_k_norm, da_lq1, da_lk1, da_lq2, da_lk2, da_subln,
              mla_wdq, mla_qa_norm, mla_wuq, mla_wdkv, mla_kv_norm, mla_wukv, mla_q_norm, mla_k_norm, mla_wo,
              peer_wq, peer_keys, peer_u, peer_v):
    xp = x_prompt
    xs = x_sample
    pos = grid_positions(xs.shape[1])
    new_da_k, new_da_v, new_ckv, new_kpe = [], [], [], []

    for l in range(DEPTH):
        p_sh1, p_sc1, p_g1, p_sh2, p_sc2, p_g2 = modulation(c_ctx[None, :], ada_w[l], ada_b[l])
        s_sh1, s_sc1, s_g1, s_sh2, s_sc2, s_g2 = modulation(c, ada_w[l], ada_b[l])
        hp = modulate(xp, norm1[l], p_sh1, p_sc1)
        hs = modulate(xs, norm1[l], s_sh1, s_sc1)
        j = l // N_MIXERS
        if l % N_MIXERS == 0:
            lam_init = 0.8 - 0.6 * float(np.exp(-0.3 * l))
            f32 = jnp.float32
            lam = (jnp.exp(jnp.sum(da_lq1[j].astype(f32) * da_lk1[j].astype(f32)))
                   - jnp.exp(jnp.sum(da_lq2[j].astype(f32) * da_lk2[j].astype(f32))) + lam_init)
            qp, kp, vp = da_qkv(hp, da_wq[j], da_wk[j], da_wv[j], da_q_norm[j], da_k_norm[j], None)
            new_da_k.append(kp)
            new_da_v.append(vp)
            op = da_out(qp, kp, vp, lam, lam_init, da_subln[j], da_wo[j])
            qs, ks_lat, vs_lat = da_qkv(hs, da_wq[j], da_wk[j], da_wv[j], da_q_norm[j], da_k_norm[j], pos)
            k_all = jnp.concatenate([ks_lat, cache_da_k[:, j].astype(ks_lat.dtype)], axis=1)
            v_all = jnp.concatenate([vs_lat, cache_da_v[:, j].astype(vs_lat.dtype)], axis=1)
            os_ = da_out(qs, k_all, v_all, lam, lam_init, da_subln[j], da_wo[j])
        else:
            qp = mla_query(hp, mla_wdq[j], mla_qa_norm[j], mla_wuq[j], mla_q_norm[j], None)
            ckv_p, kpe_p = mla_compress(hp, mla_wdkv[j], mla_kv_norm[j])
            new_ckv.append(ckv_p)
            new_kpe.append(kpe_p)
            kp, vp = mla_expand(ckv_p, kpe_p, mla_wukv[j], mla_k_norm[j], None)
            op = mla_out(qp, kp, vp, mla_wo[j])
            qs = mla_query(hs, mla_wdq[j], mla_qa_norm[j], mla_wuq[j], mla_q_norm[j], pos)
            ckv_s, kpe_s = mla_compress(hs, mla_wdkv[j], mla_kv_norm[j])
            k_lat, v_lat = mla_expand(ckv_s, kpe_s, mla_wukv[j], mla_k_norm[j], pos)
            k_ctx, v_ctx = mla_expand(cache_mla_ckv[:, j].astype(ckv_s.dtype), cache_mla_kpe[:, j].astype(kpe_s.dtype),
                                      mla_wukv[j], mla_k_norm[j], None)
            os_ = mla_out(qs, jnp.concatenate([k_lat, k_ctx], axis=1),
                          jnp.concatenate([v_lat, v_ctx], axis=1), mla_wo[j])
        xp = xp + p_g1 * op
        xs = xs + s_g1 * os_

        hp = modulate(xp, norm2[l], p_sh2, p_sc2)
        hs = modulate(xs, norm2[l], s_sh2, s_sc2)
        xp = xp + p_g2 * peer(hp, peer_wq[l], peer_keys[l], peer_u[l], peer_v[l])
        xs = xs + s_g2 * peer(hs, peer_wq[l], peer_keys[l], peer_u[l], peer_v[l])

    return (xp, xs, jnp.stack(new_da_k, axis=1), jnp.stack(new_da_v, axis=1),
            jnp.stack(new_ckv, axis=1), jnp.stack(new_kpe, axis=1))


_drawn_inputs = setup_inputs


def setup_inputs(seed=0):
    import zlib

    import numpy as np

    out = dict(_drawn_inputs(seed))
    spreads = {}
    factors = {'cache_mla_ckv': 5.084,
     'cache_mla_kpe': 7.5,
     'norm1': 2.855,
     'norm2': 3.434,
     'da_q_norm': 8.0,
     'da_k_norm': 2.854,
     'da_lq2': 5.136,
     'da_lk2': 4.009,
     'da_subln': 6.21,
     'mla_qa_norm': 8.0,
     'mla_kv_norm': 2.85,
     'mla_q_norm': 8.0,
     'mla_k_norm': 8.0,
     'cache_da_k': 8.0,
     'cache_da_v': 8.0}
    for name, (base, spread) in spreads.items():
        noise = np.random.default_rng([zlib.crc32(name.encode()), seed]).standard_normal(out[name].shape)
        drawn = base * np.exp(spread * noise) if base else spread * noise
        out[name] = __import__('jax').numpy.asarray(drawn.astype(out[name].dtype))
    for name, factor in factors.items():
        out[name] = (out[name] * factor).astype(out[name].dtype)
    return out
```

```python
from contextlib import ExitStack

import numpy as np

import concourse.bass as bass
from concourse import mybir

F32 = mybir.dt.float32
U32 = mybir.dt.uint32
ALU = mybir.AluOpType
ACT = mybir.ActivationFunctionType
AX = mybir.AxisListType.X

P = 128
D = 1024
DC = D // P
TS, TP, TC = 512, 128, 128
T = TS + TP
TK = T + TC
SEG = ((0, 0, TS), (1, TS, T))
EPS = 1e-6
HDA, DDA, VDA = 8, 64, 128
HM, DN, DR, DV = 16, 64, 32, 64
DQ = DN + DR
GH = HM // 2
QL, KL = 512, 256
HP, NK, TOPK = 8, 128, 16
HC = 2 * HP
NG = 4
GROUPS = NK // NG
TB = T // P
BT = 32
NEG = -3.0e38
SLOTS = 3

J_ADA = (0, 12)
J_WQ, J_WK, J_WV, J_WO0 = 24, 26, 28, 30
J_PQ = (32, 44)
J_WDQ, J_WDKV, J_GROUP, J_WO1 = 36, 37, 38, 42
N_CHUNKS = 48


def mixed(nc, cst, inp, outs, g_dram):
    es = ExitStack()
    sems = {}

    def sem(name):
        if name not in sems:
            sems[name] = es.enter_context(nc.semaphore(name))
        return sems[name]

    def sb(stack, name, shape, dt=F32):
        return stack.enter_context(nc.sbuf_tensor(name, shape, dt))

    xT = sb(es, "xT", [P, DC, T])
    hT = sb(es, "hT", [P, DC, T])
    mod = sb(es, "mod", [P, 2, 48, 2])
    ada_b = sb(es, "ada_b", [P, 2, 48])
    c_in = sb(es, "c_in", [P, DC, 2])
    c_silu = sb(es, "c_silu", [P, DC, 2])
    norms = sb(es, "norms", [P, 4, DC])
    gains = sb(es, "gains", [P, 16])
    lam_in = sb(es, "lam_in", [P, 4, DDA])
    lam = sb(es, "lam", [P, 8])
    consts = sb(es, "consts", [P, 5, P])
    ind = sb(es, "ind", [P, 3, 8, 16])
    indT = sb(es, "indT", [16, 2, 8, P])
    iota = sb(es, "iota", [P, P])
    eps = sb(es, "eps", [P, 1])
    small = sb(es, "small", [P, 64])
    ring = sb(es, "ring", [P, SLOTS, 4096])
    ps = es.enter_context(nc.psum_tensor("ps", [P, 8, 512], F32))

    ones, ident, rot_da, rot_mla, place = (consts[:, k, :] for k in range(5))

    def bank2(b, n=T, p=P):
        return ps[0:p, b:b + 2, :].rearrange("p a n -> p (a n)")[:, 0:n]

    def product(e, out, lhsT, rhs, start, stop):
        n = rhs.shape[-1]
        e.matmul(out[:, 0:512], lhsT, rhs[:, 0:512], start=start, stop=stop)
        return e.matmul(out[:, 512:n], lhsT, rhs[:, 512:n], start=start, stop=stop)

    def chunk_in(e, j):
        e.wait_ge(sem(f"chunk_in{j % SLOTS}"), 16 * (j // SLOTS + 1))

    def load_chunk(sp, ring, j, read):
        if j - SLOTS in read:
            sp.wait_ge(*read[j - SLOTS])
        sp.dma_start(ring[:, j % SLOTS, :], inp["wts"][j]).then_inc(sem(f"chunk_in{j % SLOTS}"), 16)

    def modulation(ring):
        with nc.Block() as block:
            @block.sync
            def _(sp):
                for name, t in (("c_in", c_in), ("norms", norms), ("gains", gains), ("lam_in", lam_in),
                                ("consts", consts), ("ada_b", ada_b), ("ind", ind), ("iota", iota), ("xT", xT)):
                    sp.dma_start(t[:], inp[name]).then_inc(sem("inputs_in"), 16)
                sp.dma_start(indT[:], inp["indT"]).then_inc(sem("inputs_in"), 16)
                for j in range(SLOTS):
                    sp.dma_start(ring[:, j, :], inp["wts"][j]).then_inc(sem(f"chunk_in{j}"), 16)
                with sp.Fori(1, 24 // SLOTS) as i:
                    for s in range(SLOTS):
                        sp.wait_ge(sem("ada_mm"), i * SLOTS + (s - SLOTS + 1))
                        src = inp["wts"][bass.ds(i * SLOTS + s, 1)].rearrange("a p n -> p (a n)")
                        sp.dma_start(ring[:, s, :], src).then_inc(sem(f"chunk_in{s}"), 16)

            @block.scalar
            def _(act):
                act.wait_ge(sem("inputs_in"), 160)
                act.activation(c_silu[:], c_in[:], ACT.Silu).then_inc(sem("silu"), 1)

            @block.tensor
            def _(pe):
                pe.wait_ge(sem("silu"), 1)
                with pe.Fori(0, 24 // SLOTS) as i:
                    for s in range(SLOTS):
                        pe.wait_ge(sem(f"chunk_in{s}"), (i + 1) * 16)
                        w = ring[:, s, :].rearrange("p (c n) -> p c n", c=DC)
                        for nb in range(4):
                            out = ps[:, 0, bass.ds((i * SLOTS + s) * 8 + 2 * nb, 2)]
                            for dc in range(DC):
                                mm = pe.matmul(out, w[:, dc, nb * P:(nb + 1) * P], c_silu[:, dc, :],
                                               start=dc == 0, stop=dc == DC - 1)
                        mm.then_inc(sem("ada_mm"), 1)

            @block.vector
            def _(v):
                v.memset(eps[:], EPS).then_inc(sem("eps_set"), 1)
                s = sem("mod_v")
                v.wait_ge(sem("inputs_in"), 160)
                v.tensor_tensor(lam_in[:, 0, :], lam_in[:, 0, :], lam_in[:, 1, :], ALU.mult).then_inc(s, 1)
                v.tensor_tensor(lam_in[:, 2, :], lam_in[:, 2, :], lam_in[:, 3, :], ALU.mult).then_inc(s, 1)
                v.wait_ge(s, 2)
                v.tensor_reduce(lam[:, 0:1], lam_in[:, 0, :], AX, ALU.add).then_inc(s, 1)
                v.tensor_reduce(lam[:, 1:2], lam_in[:, 2, :], AX, ALU.add).then_inc(s, 1)
                v.wait_ge(sem("lam_exp"), 1)
                v.tensor_tensor(lam[:, 2:3], lam[:, 1:2], lam[:, 0:1], ALU.subtract).then_inc(s, 1)
                v.wait_ge(s, 5)
                v.tensor_scalar(lam[:, 4:5], lam[:, 2:3], -LAM_INIT, None, ALU.add).then_inc(s, 1)
                v.tensor_scalar(gains[:, 2:3], gains[:, 2:3], 1.0 - LAM_INIT, None, ALU.mult).then_inc(s, 1)
                v.wait_ge(sem("ada_mm"), 24)
                v.tensor_tensor(mod[:].rearrange("p l k c -> p (l k) c"),
                                ps[:, 0, 0:192].rearrange("p (k c) -> p k c", c=2),
                                ada_b[:].rearrange("p l k -> p (l k)").unsqueeze(2).to_broadcast([P, 96, 2]),
                                ALU.add).then_inc(s, 1)
                v.wait_ge(s, 8)
                for l in range(2):
                    for half in range(2):
                        m = mod[:, l, 24 * half + 8:24 * half + 16, :]
                        g = norms[:, 2 * half + l, :].unsqueeze(2).to_broadcast([P, DC, 2])
                        v.scalar_tensor_tensor(m, m, 1.0, g, ALU.add, ALU.mult).then_inc(s, 1)

            @block.scalar
            def _(act):
                act.wait_ge(sem("mod_v"), 4)
                act.activation(lam[:, 0:2], lam[:, 0:2], ACT.Exp).then_inc(sem("lam_exp"), 1)

    def norm(l, half, sq):
        n = f"norm{l}{half}_"
        with nc.Block() as block:
            @block.scalar
            def _(act):
                for k in range(DC):
                    act.activation(sq[:, k, :], xT[:, k, :], ACT.Square).then_inc(sem(n + "sq"), 1)
                act.wait_ge(sem(n + "mm"), 1)
                act.activation(sq[:, 0, :], bank2(0), ACT.Sqrt, bias=eps[:], scale=1.0 / D).then_inc(sem(n + "sd"), 1)
                for k in range(DC):
                    for c, a, b in SEG:
                        act.wait_ge(sem(n + "v"), 1 + 2 * k + c + 1)
                        act.activation(hT[:, k, a:b], hT[:, k, a:b], ACT.Identity,
                                       bias=mod[:, l, 24 * half + k, c:c + 1])

            @block.tensor
            def _(pe):
                for k in range(DC):
                    pe.wait_ge(sem(n + "sq"), k + 1)
                    mm = product(pe, bank2(0), ones, sq[:, k, :], k == 0, k == DC - 1)
                mm.then_inc(sem(n + "mm"), 1)

            @block.vector
            def _(v):
                v.wait_ge(sem(n + "sd"), 1)
                v.reciprocal(sq[:, 1, :], sq[:, 0, :]).then_inc(sem(n + "v"), 1)
                v.wait_ge(sem(n + "v"), 1)
                for k in range(DC):
                    for c, a, b in SEG:
                        v.scalar_tensor_tensor(hT[:, k, a:b], xT[:, k, a:b],
                                               mod[:, l, 24 * half + 8 + k, c:c + 1], sq[:, 1, a:b],
                                               ALU.mult, ALU.mult).then_inc(sem(n + "v"), 1)

    def diff_qkv(ring, qT, kT, V, cos, sin, scr):
        rs = scr[:, 0, :]
        with nc.Block() as block:
            @block.sync
            def _(sp):
                sp.dma_start(cos[:], inp["cos_da"]).then_inc(sem("da_in"), 16)
                sp.dma_start(sin[:], inp["sin_da"]).then_inc(sem("da_in"), 16)
                sp.dma_start(V[:, 5, :], inp["cache_v"]).then_inc(sem("da_in"), 16)
                sp.dma_start(kT[:, :, T:TK], inp["cache_k"]).then_inc(sem("da_in"), 16)
                read = {24 + c: (sem("qk_mm"), 4 * (c + 1)) for c in range(4)}
                read |= {28 + c: (sem("v_mm"), 5 * (c + 1)) for c in range(2)}
                for j in range(24, 30):
                    load_chunk(sp, ring, j, read)
                for c in range(2):
                    load_chunk(sp, ring, 30 + c, read)
                sp.wait_ge(sem("rot_v"), 4 * 16)
                sp.dma_start(outs["da_k"], kT[:, :, TS:T]).then_inc(sem("stored"), 16)
                sp.wait_ge(sem("v_copied"), 10)
                sp.dma_start(outs["da_v"], V[:, 4, :]).then_inc(sem("stored"), 16)
                sp.wait_ge(sem("stored"), 32)

            @block.tensor
            def _(pe):
                def squares(i):
                    which, nb = divmod(i, 8)
                    pe.wait_ge(sem("qk_a"), 2 * (i + 1))
                    product(pe, bank2(4 + 2 * which, T, 16), ind[:, 0, nb, :], scr[:, 1 + i % 2, :],
                            nb == 0, nb == 7).then_inc(sem("sq_mm"), 1)

                for i in range(16):
                    j = 24 + i // 4
                    if i % 4 == 0:
                        chunk_in(pe, j)
                    if i >= 2:
                        pe.wait_ge(sem("qk_a"), 2 * (i - 1))
                    w = ring[:, j % SLOTS, :].rearrange("p (c n) -> p c n", c=DC)
                    for dc in range(DC):
                        mm = product(pe, bank2(2 * (i % 2)), w[:, dc, (i % 4) * P:(i % 4 + 1) * P], hT[:, dc, :],
                                     dc == 0, dc == DC - 1)
                    mm.then_inc(sem("qk_mm"), 1)
                    if i >= 1:
                        squares(i - 1)
                squares(15)
                for i in range(10):
                    c, tb = divmod(i, 5)
                    if tb == 0:
                        chunk_in(pe, 28 + c)
                    if i < 4:
                        pe.wait_ge(sem("qk_a"), 32)
                    else:
                        pe.wait_ge(sem("v_copied"), i - 3)
                    w = ring[:, (28 + c) % SLOTS, :].rearrange("p (c n) -> p c n", c=DC)
                    for dc in range(DC):
                        mm = pe.matmul(ps[:, i % 4, :], hT[:, dc, tb * P:(tb + 1) * P], w[:, dc, :],
                                       start=dc == 0, stop=dc == DC - 1)
                    mm.then_inc(sem("v_mm"), 1)
                pe.wait_ge(sem("v_copied"), 10)
                pe.wait_ge(sem("rs_v"), 2)
                for i in range(16):
                    which, nb = divmod(i, 8)
                    b = 4 * (i % 2)
                    if i >= 2:
                        pe.wait_ge(sem("rot_v"), 4 * (i - 1))
                    t = (qT, kT)[which]
                    product(pe, bank2(b), rot_da, t[:, nb, 0:T], True, True)
                    product(pe, bank2(b + 2), indT[:, 0, nb, :], rs[32 * which:32 * which + 16, :] if which == 0 else scr[0:16, 3, :],
                            True, True).then_inc(sem("rot_mm"), 1)

            @block.scalar
            def _(act):
                for i in range(16):
                    which, nb = divmod(i, 8)
                    act.wait_ge(sem("qk_mm"), i + 1)
                    act.activation((qT, kT)[which][:, nb, 0:T], bank2(2 * (i % 2)), ACT.Identity,
                                   scale=gains[:, which:which + 1]).then_inc(sem("qk_a"), 1)
                    if i >= 2:
                        act.wait_ge(sem("sq_mm"), i - 1)
                    act.activation(scr[:, 1 + i % 2, :], bank2(2 * (i % 2)), ACT.Square).then_inc(sem("qk_a"), 1)
                for which in range(2):
                    act.wait_ge(sem("sq_mm"), 8 * (which + 1))
                    act.activation(scr[0:16, 4 + which, :], bank2(4 + 2 * which, T, 16), ACT.Sqrt,
                                   bias=eps[0:16], scale=1.0 / DDA).then_inc(sem("sd_a"), 1)
                for i in range(10):
                    c, tb = divmod(i, 5)
                    act.wait_ge(sem("v_mm"), i + 1)
                    act.copy(V[:, tb, c * 512:(c + 1) * 512], ps[:, i % 4, :]).then_inc(sem("v_copied"), 1)

            @block.vector
            def _(v):
                for which in range(2):
                    v.wait_ge(sem("sd_a"), which + 1)
                    v.reciprocal(scr[0:16, 3 * which, :], scr[0:16, 4 + which, :]).then_inc(sem("rs_v"), 1)
                v.wait_ge(sem("da_in"), 64)
                n = 0
                for i in range(16):
                    which, nb = divmod(i, 8)
                    b = 4 * (i % 2)
                    t = (qT, kT)[which][:, nb, 0:T]
                    turned = scr[:, 1 + i % 2, :]
                    v.wait_ge(sem("rot_mm"), i + 1)
                    v.tensor_tensor(turned, bank2(b), sin[:, 0:T], ALU.mult).then_inc(sem("rot_v"), 1)
                    v.tensor_tensor(t, t, cos[:, 0:T], ALU.mult).then_inc(sem("rot_v"), 1)
                    n += 2
                    v.wait_ge(sem("rot_v"), n)
                    v.tensor_tensor(t, t, turned, ALU.add).then_inc(sem("rot_v"), 1)
                    n += 1
                    v.wait_ge(sem("rot_v"), n)
                    v.tensor_tensor(t, t, bank2(b + 2), ALU.mult).then_inc(sem("rot_v"), 1)
                    n += 1

    def diff_attention(qT, kT, V, oT, pr, pT):
        items = [(hd, qb) for hd in range(HDA) for qb in range(TB)]
        scale = DDA ** -0.5

        def width(qb):
            return T if qb < 4 else TP

        with nc.Block() as block:
            @block.tensor
            def _(pe):
                def scores(w):
                    hd, qb = items[w]
                    for c in range(2):
                        q = qT[64 * c:64 * c + 64, hd, qb * P:(qb + 1) * P]
                        k = kT[64 * c:64 * c + 64, hd, :]
                        if w:
                            pe.wait_ge(sem("da_exp"), 2 * (w - 1) + c + 1)
                        if qb < 4:
                            pe.matmul(ps[:, 2 * c, :], q, k[:, 0:TS], start=True, stop=True)
                            mm = pe.matmul(ps[:, 2 * c + 1, 0:TC], q, k[:, T:TK], start=True, stop=True)
                        else:
                            mm = pe.matmul(ps[:, 2 * c, 0:TP], q, k[:, TS:T], start=True, stop=True)
                        mm.then_inc(sem("da_s"), 1)

                def values(w):
                    hd, qb = items[w]
                    blocks = (0, 1, 2, 3, 5) if qb < 4 else (4,)
                    pe.wait_ge(sem("da_w"), 8 * (w + 1))
                    if w >= 1:
                        pe.wait_ge(sem("da_pT"), w)
                    for k in range(len(blocks)):
                        mm = pe.transpose(bank2(4)[:, k * P:(k + 1) * P], pr[:, w % 2, 0, k * P:(k + 1) * P], ident)
                    mm.then_inc(sem("da_t"), 1)
                    pe.wait_ge(sem("da_pT"), w + 1)
                    if w >= 2:
                        pe.wait_ge(sem("da_o"), w - 1)
                    for k, kb in enumerate(blocks):
                        mm = pe.matmul(ps[:, 6 + w % 2, 0:P], V[:, kb, hd * P:(hd + 1) * P], pT[:, w % 2, k * P:(k + 1) * P],
                                       start=k == 0, stop=k == len(blocks) - 1)
                    mm.then_inc(sem("da_pv"), 1)

                for w in range(len(items)):
                    scores(w)
                    if w:
                        values(w - 1)
                values(len(items) - 1)

            @block.vector
            def _(v):
                s = sem("da_w")
                for w, (hd, qb) in enumerate(items):
                    n, k0 = width(qb), 8 * w
                    z = small[:, 16 * (w % 2):16 * (w % 2) + 16]
                    for c in range(2):
                        v.wait_ge(sem("da_s"), 2 * w + c + 1)
                        v.tensor_reduce(z[:, c:c + 1], bank2(2 * c, n), AX, ALU.max).then_inc(s, 1)
                        v.wait_ge(s, k0 + 2 * c + 1)
                        v.tensor_scalar(z[:, 2 + c:3 + c], z[:, c:c + 1], -scale, None, ALU.mult).then_inc(s, 1)
                    v.wait_ge(sem("da_exp"), 2 * w + 2)
                    v.reciprocal(z[:, 6:8], z[:, 4:6]).then_inc(s, 1)
                    v.wait_ge(s, k0 + 5)
                    v.tensor_tensor(z[:, 8:9], z[:, 7:8], lam[:, 4:5], ALU.mult).then_inc(s, 1)
                    p0, p1 = pr[:, w % 2, 0, 0:n], pr[:, w % 2, 1, 0:n]
                    v.tensor_scalar(p0, p0, z[:, 6:7], None, ALU.mult).then_inc(s, 1)
                    v.wait_ge(s, k0 + 7)
                    v.scalar_tensor_tensor(p0, p1, z[:, 8:9], p0, ALU.mult, ALU.add).then_inc(s, 1)

            @block.scalar
            def _(act):
                def exps(w):
                    hd, qb = items[w]
                    n = width(qb)
                    z = small[:, 16 * (w % 2):16 * (w % 2) + 16]
                    if w >= 2:
                        act.wait_ge(sem("da_t"), w - 1)
                    for c in range(2):
                        act.wait_ge(sem("da_w"), 8 * w + 2 * c + 2)
                        act.activation(pr[:, w % 2, c, 0:n], bank2(2 * c, n), ACT.Exp, bias=z[:, 2 + c:3 + c],
                                       scale=scale, accum_out=z[:, 4 + c:5 + c]).then_inc(sem("da_exp"), 1)

                def copies(w):
                    hd, qb = items[w]
                    n = width(qb)
                    act.wait_ge(sem("da_t"), w + 1)
                    if w >= 2:
                        act.wait_ge(sem("da_pv"), w - 1)
                    act.copy(pT[:, w % 2, 0:n], bank2(4, n)).then_inc(sem("da_pT"), 1)
                    act.wait_ge(sem("da_pv"), w + 1)
                    act.copy(oT[:, hd, qb * P:(qb + 1) * P], ps[:, 6 + w % 2, 0:P]).then_inc(sem("da_o"), 1)

                for w in range(len(items)):
                    exps(w)
                    if w:
                        copies(w - 1)
                copies(len(items) - 1)

    def diff_subnorm(oT, scr):
        with nc.Block() as block:
            @block.scalar
            def _(act):
                for h in range(HDA):
                    if h >= 2:
                        act.wait_ge(sem("sub_mm"), h - 1)
                    act.activation(scr[:, 1 + h % 2, :], oT[:, h, :], ACT.Square).then_inc(sem("sub_sq"), 1)
                act.wait_ge(sem("sub_mm"), HDA)
                act.activation(scr[0:16, 0, :], bank2(0, T, 16), ACT.Sqrt, bias=eps[0:16], scale=1.0 / VDA)\
                   .then_inc(sem("sub_sd"), 1)

            @block.tensor
            def _(pe):
                for h in range(HDA):
                    pe.wait_ge(sem("sub_sq"), h + 1)
                    product(pe, bank2(0, T, 16), ind[:, 1, h, :], scr[:, 1 + h % 2, :], h == 0, h == HDA - 1)\
                        .then_inc(sem("sub_mm"), 1)
                pe.wait_ge(sem("sub_v"), 1)
                for h in range(HDA):
                    if h >= 3:
                        pe.wait_ge(sem("sub_v"), h - 1)
                    product(pe, bank2(2 + 2 * (h % 3)), indT[:, 1, h, :], scr[0:16, 3, :], True, True)\
                        .then_inc(sem("sub_bc"), 1)

            @block.vector
            def _(v):
                v.wait_ge(sem("sub_sd"), 1)
                v.reciprocal(scr[0:16, 3, :], scr[0:16, 0, :]).then_inc(sem("sub_v"), 1)
                for h in range(HDA):
                    v.wait_ge(sem("sub_bc"), h + 1)
                    v.scalar_tensor_tensor(oT[:, h, :], oT[:, h, :], gains[:, 2:3], bank2(2 + 2 * (h % 3)),
                                           ALU.mult, ALU.mult).then_inc(sem("sub_v"), 1)

    def out_product(l, ring, oT, j0, nxt):
        n = f"wo{l}_"
        with nc.Block() as block:
            @block.sync
            def _(sp):
                read = {j0 + c: (sem(n + "mm"), 4 * (c + 1)) for c in range(2)}
                for j in nxt:
                    load_chunk(sp, ring, j, read)

            @block.tensor
            def _(pe):
                for nb in range(DC):
                    j = j0 + nb // 4
                    if nb % 4 == 0:
                        chunk_in(pe, j)
                    if nb >= 4:
                        pe.wait_ge(sem(n + "v"), 2 * (nb - 3))
                    w = ring[:, j % SLOTS, :].rearrange("p (c n) -> p c n", c=DC)
                    for c in range(DC):
                        mm = product(pe, bank2(2 * (nb % 4)), w[:, c, (nb % 4) * P:(nb % 4 + 1) * P], oT[:, c, :],
                                     c == 0, c == DC - 1)
                    mm.then_inc(sem(n + "mm"), 1)

            @block.vector
            def _(v):
                for nb in range(DC):
                    v.wait_ge(sem(n + "mm"), nb + 1)
                    for c, a, b in SEG:
                        v.scalar_tensor_tensor(xT[:, nb, a:b], bank2(2 * (nb % 4))[:, a:b], mod[:, l, 16 + nb, c:c + 1],
                                               xT[:, nb, a:b], ALU.mult, ALU.add).then_inc(sem(n + "v"), 1)

    def mla_compress(ring, cqT, ckvT, kpeT, cos, sin, scr):
        parts = [("q", nb) for nb in range(4)] + [("kv", nb) for nb in range(3)]
        with nc.Block() as block:
            @block.sync
            def _(sp):
                sp.dma_start(cos[:], inp["cos_mla"]).then_inc(sem("mla_in"), 16)
                sp.dma_start(sin[:], inp["sin_mla"]).then_inc(sem("mla_in"), 16)
                sp.dma_start(ckvT[:, :, T:TK], inp["cache_ckv"]).then_inc(sem("mla_in"), 16)
                sp.dma_start(kpeT[:, T:TK], inp["cache_kpe"]).then_inc(sem("mla_in"), 16)
                read = {J_WDQ: (sem("cmp_mm"), 4), J_WDKV: (sem("cmp_mm"), 7)}
                load_chunk(sp, ring, J_GROUP, read)
                load_chunk(sp, ring, J_GROUP + 1, read)
                load_chunk(sp, ring, J_GROUP + 2, read)
                sp.wait_ge(sem("cmp_v"), 2 + 4 + 2)
                sp.dma_start(outs["ckv"], ckvT[:, :, TS:T]).then_inc(sem("stored"), 16)
                sp.wait_ge(sem("cmp_a"), 2 * 6 + 1)
                sp.dma_start(outs["kpe"], kpeT[:, TS:T]).then_inc(sem("stored"), 16)
                sp.wait_ge(sem("stored"), 64)
                sp.wait_ge(sem("mla_in"), 64)

            @block.tensor
            def _(pe):
                def squares(i):
                    which, nb = parts[i]
                    pe.wait_ge(sem("cmp_a"), 2 * (i + 1))
                    product(pe, bank2(4 if which == "q" else 6), ones, scr[:, 1 + i % 2, :], nb == 0,
                            nb == (3 if which == "q" else 1)).then_inc(sem("cmp_sq"), 1)

                for i, (which, nb) in enumerate(parts):
                    j = J_WDQ if which == "q" else J_WDKV
                    if nb == 0:
                        chunk_in(pe, j)
                    if i >= 2:
                        pe.wait_ge(sem("cmp_a"), 2 * (i - 1))
                    w = ring[:, j % SLOTS, :].rearrange("p (c n) -> p c n", c=DC)
                    m = P if i < 6 else DR
                    for dc in range(DC):
                        mm = product(pe, bank2(2 * (i % 2), T, m), w[:, dc, nb * P:nb * P + m], hT[:, dc, :],
                                     dc == 0, dc == DC - 1)
                    mm.then_inc(sem("cmp_mm"), 1)
                    if i >= 1:
                        squares(i - 1)

            @block.scalar
            def _(act):
                for i, (which, nb) in enumerate(parts):
                    act.wait_ge(sem("cmp_mm"), i + 1)
                    src = bank2(2 * (i % 2))
                    if i == 6:
                        act.copy(kpeT[:, 0:T], bank2(0, T, DR)).then_inc(sem("cmp_a"), 1)
                        continue
                    dst = cqT[:, nb, :] if which == "q" else ckvT[:, nb, 0:T]
                    g = 3 + nb if which == "q" else 7 + nb
                    act.activation(dst, src, ACT.Identity, scale=gains[:, g:g + 1]).then_inc(sem("cmp_a"), 1)
                    if i >= 2:
                        act.wait_ge(sem("cmp_sq"), i - 1)
                    act.activation(scr[:, 1 + i % 2, :], src, ACT.Square).then_inc(sem("cmp_a"), 1)
                act.wait_ge(sem("cmp_sq"), 6)
                act.activation(scr[:, 0, :], bank2(4), ACT.Sqrt, bias=eps[:], scale=1.0 / QL).then_inc(sem("cmp_sd"), 1)
                act.activation(scr[:, 3, :], bank2(6), ACT.Sqrt, bias=eps[:], scale=1.0 / KL).then_inc(sem("cmp_sd"), 1)

            @block.vector
            def _(v):
                s = sem("cmp_v")
                v.wait_ge(sem("cmp_sd"), 2)
                v.reciprocal(scr[:, 0, :], scr[:, 0, :]).then_inc(s, 1)
                v.reciprocal(scr[:, 3, :], scr[:, 3, :]).then_inc(s, 1)
                v.wait_ge(s, 2)
                for nb in range(2):
                    v.tensor_tensor(ckvT[:, nb, 0:T], ckvT[:, nb, 0:T], scr[:, 3, :], ALU.mult).then_inc(s, 1)
                for nb in range(4):
                    v.tensor_tensor(cqT[:, nb, :], cqT[:, nb, :], scr[:, 0, :], ALU.mult).then_inc(s, 1)

    def mla_heads(g, ring, cqT, ckvT, kpeT, qT, kT, V, cos, sin, scr, xk):
        n = f"mh{g}_"
        jq, jk = J_GROUP + 2 * g, J_GROUP + 2 * g + 1
        wq = ring[:, jq % SLOTS, :].rearrange("p (c n) -> p c n", c=4)
        wk = ring[:, jk % SLOTS, 0:2 * GH * DQ].rearrange("p (c n) -> p c n", c=2)
        wv = ring[:, jk % SLOTS, 2 * GH * DQ:2 * GH * (DQ + DV)].rearrange("p (c n) -> p c n", c=2)
        items = [(0, h) for h in range(GH)] + [(1, h) for h in range(GH)]
        cols = (T, TK)
        with nc.Block() as block:
            @block.sync
            def _(sp):
                if g == 0:
                    load_chunk(sp, ring, J_GROUP + 3, {J_GROUP: (sem(n + "mm"), GH)})
                else:
                    load_chunk(sp, ring, J_WO1, {})
                    load_chunk(sp, ring, J_WO1 + 1, {J_GROUP + 2: (sem(n + "mm"), GH)})

            @block.tensor
            def _(pe):
                def squares(i):
                    which, h = items[i]
                    pe.wait_ge(sem(n + "a"), 2 * (i + 1))
                    product(pe, bank2(4 + 2 * which, cols[which], 16), ind[0:DQ, 2, h, :], xk[0:DQ, i % 2, 0:cols[which]],
                            h == 0, h == GH - 1).then_inc(sem(n + "sq"), 1)

                chunk_in(pe, jq)
                chunk_in(pe, jk)
                for i, (which, h) in enumerate(items):
                    if i >= 2:
                        pe.wait_ge(sem(n + "a"), 2 * (i - 1))
                    b = 2 * (i % 2)
                    if which == 0:
                        for c in range(4):
                            mm = product(pe, bank2(b, T, DQ), wq[:, c, h * DQ:(h + 1) * DQ], cqT[:, c, :], c == 0, c == 3)
                    else:
                        product(pe, bank2(b, TK, DQ), place[0:DR, 0:DQ], kpeT[:, :], True, False)
                        for c in range(2):
                            mm = product(pe, bank2(b, TK, DQ), wk[:, c, h * DQ:(h + 1) * DQ], ckvT[:, c, :], False, c == 1)
                    mm.then_inc(sem(n + "mm"), 1)
                    if i >= 1:
                        squares(i - 1)
                squares(15)
                for i in range(6):
                    if i < 4:
                        pe.wait_ge(sem(n + "a"), 32)
                    else:
                        pe.wait_ge(sem(n + "vc"), i - 3)
                    for c in range(2):
                        mm = pe.matmul(ps[:, i % 4, :], ckvT[:, c, i * P:(i + 1) * P], wv[:, c], start=c == 0, stop=c == 1)
                    mm.then_inc(sem(n + "vm"), 1)
                pe.wait_ge(sem(n + "vc"), 6)
                pe.wait_ge(sem(n + "rs"), 2)
                for i, (which, h) in enumerate(items):
                    b = 4 * (i % 2)
                    if i >= 2:
                        pe.wait_ge(sem(n + "v"), 4 * (i - 1))
                    t, m = (qT, kT)[which], cols[which]
                    product(pe, bank2(b, m, DQ), rot_mla[0:DQ, 0:DQ], t[0:DQ, h, 0:m], True, True)
                    product(pe, bank2(b + 2, m, DQ), indT[:, 1, h, 0:DQ], scr[0:16, which, 0:m], True, True)\
                        .then_inc(sem(n + "rm"), 1)

            @block.scalar
            def _(act):
                for i, (which, h) in enumerate(items):
                    m = cols[which]
                    act.wait_ge(sem(n + "mm"), i + 1)
                    act.activation((qT, kT)[which][0:DQ, h, 0:m], bank2(2 * (i % 2), m, DQ), ACT.Identity,
                                   scale=gains[0:DQ, 9 + which:10 + which]).then_inc(sem(n + "a"), 1)
                    if i >= 2:
                        act.wait_ge(sem(n + "sq"), i - 1)
                    act.activation(xk[0:DQ, i % 2, 0:m], bank2(2 * (i % 2), m, DQ), ACT.Square).then_inc(sem(n + "a"), 1)
                for which in range(2):
                    m = cols[which]
                    act.wait_ge(sem(n + "sq"), 8 * (which + 1))
                    act.activation(scr[0:16, 2 + which, 0:m], bank2(4 + 2 * which, m, 16), ACT.Sqrt, bias=eps[0:16],
                                   scale=1.0 / DQ).then_inc(sem(n + "sd"), 1)
                for i in range(6):
                    act.wait_ge(sem(n + "vm"), i + 1)
                    act.copy(V[:, i, :], ps[:, i % 4, :]).then_inc(sem(n + "vc"), 1)

            @block.vector
            def _(v):
                for which in range(2):
                    m = cols[which]
                    v.wait_ge(sem(n + "sd"), which + 1)
                    v.reciprocal(scr[0:16, which, 0:m], scr[0:16, 2 + which, 0:m]).then_inc(sem(n + "rs"), 1)
                k = 0
                for i, (which, h) in enumerate(items):
                    b, m = 4 * (i % 2), cols[which]
                    t = (qT, kT)[which][0:DQ, h, 0:m]
                    turned = xk[0:DQ, i % 2, 0:m]
                    v.wait_ge(sem(n + "rm"), i + 1)
                    v.tensor_tensor(turned, bank2(b, m, DQ), sin[0:DQ, 0:m], ALU.mult).then_inc(sem(n + "v"), 1)
                    v.tensor_tensor(t, t, cos[0:DQ, 0:m], ALU.mult).then_inc(sem(n + "v"), 1)
                    k += 2
                    v.wait_ge(sem(n + "v"), k)
                    v.tensor_tensor(t, t, turned, ALU.add).then_inc(sem(n + "v"), 1)
                    k += 1
                    v.wait_ge(sem(n + "v"), k)
                    v.tensor_tensor(t, t, bank2(b + 2, m, DQ), ALU.mult).then_inc(sem(n + "v"), 1)
                    k += 1

    def mla_attention(g, qT, kT, V, oT, pr, pT):
        items = [(h, qb) for h in range(GH) for qb in range(TB)]
        scale = DQ ** -0.5
        n_ = f"ma{g}_"

        def width(qb):
            return T if qb < 4 else TP

        with nc.Block() as block:
            @block.tensor
            def _(pe):
                def scores(w):
                    h, qb = items[w]
                    q, k, b = qT[0:DQ, h, qb * P:(qb + 1) * P], kT[0:DQ, h, :], 2 * (w % 2)
                    if w >= 2:
                        pe.wait_ge(sem(n_ + "exp"), w - 1)
                    if qb < 4:
                        pe.matmul(ps[:, b, :], q, k[:, 0:TS], start=True, stop=True)
                        mm = pe.matmul(ps[:, b + 1, 0:TC], q, k[:, T:TK], start=True, stop=True)
                    else:
                        mm = pe.matmul(ps[:, b, 0:TP], q, k[:, TS:T], start=True, stop=True)
                    mm.then_inc(sem(n_ + "s"), 1)

                def values(w):
                    h, qb = items[w]
                    blocks = (0, 1, 2, 3, 5) if qb < 4 else (4,)
                    pe.wait_ge(sem(n_ + "w"), 4 * (w + 1))
                    if w >= 1:
                        pe.wait_ge(sem(n_ + "pT"), w)
                    for k in range(len(blocks)):
                        mm = pe.transpose(bank2(4)[:, k * P:(k + 1) * P], pr[:, w % 2, 0, k * P:(k + 1) * P], ident)
                    mm.then_inc(sem(n_ + "t"), 1)
                    pe.wait_ge(sem(n_ + "pT"), w + 1)
                    if w >= 2:
                        pe.wait_ge(sem(n_ + "o"), w - 1)
                    for k, kb in enumerate(blocks):
                        mm = pe.matmul(ps[:, 6 + w % 2, 0:P], V[:, kb, (h // 2) * P:(h // 2 + 1) * P],
                                       pT[:, w % 2, k * P:(k + 1) * P], start=k == 0, stop=k == len(blocks) - 1)
                    mm.then_inc(sem(n_ + "pv"), 1)

                for w in range(len(items)):
                    scores(w)
                    if w:
                        values(w - 1)
                values(len(items) - 1)

            @block.vector
            def _(v):
                s = sem(n_ + "w")

                def maxima(w):
                    n = width(items[w][1])
                    z = small[:, 16 * (w % 2):16 * (w % 2) + 16]
                    v.wait_ge(sem(n_ + "s"), w + 1)
                    v.tensor_reduce(z[:, 0:1], bank2(2 * (w % 2), n), AX, ALU.max).then_inc(s, 1)
                    v.wait_ge(s, 4 * w + 1)
                    v.tensor_scalar(z[:, 2:3], z[:, 0:1], -scale, None, ALU.mult).then_inc(s, 1)

                def weights(w):
                    n = width(items[w][1])
                    z = small[:, 16 * (w % 2):16 * (w % 2) + 16]
                    v.wait_ge(sem(n_ + "exp"), w + 1)
                    v.reciprocal(z[:, 6:7], z[:, 4:5]).then_inc(s, 1)
                    v.wait_ge(s, 4 * w + 3)
                    p0 = pr[:, w % 2, 0, 0:n]
                    v.tensor_scalar(p0, p0, z[:, 6:7], None, ALU.mult).then_inc(s, 1)

                for w in range(len(items)):
                    maxima(w)
                    weights(w)

            @block.scalar
            def _(act):
                def exps(w):
                    n = width(items[w][1])
                    z = small[:, 16 * (w % 2):16 * (w % 2) + 16]
                    if w >= 2:
                        act.wait_ge(sem(n_ + "t"), w - 1)
                    act.wait_ge(sem(n_ + "w"), 4 * w + 2)
                    act.activation(pr[:, w % 2, 0, 0:n], bank2(2 * (w % 2), n), ACT.Exp, bias=z[:, 2:3],
                                   scale=scale, accum_out=z[:, 4:5]).then_inc(sem(n_ + "exp"), 1)

                def copies(w):
                    h, qb = items[w]
                    n = width(qb)
                    act.wait_ge(sem(n_ + "t"), w + 1)
                    if w >= 2:
                        act.wait_ge(sem(n_ + "pv"), w - 1)
                    act.copy(pT[:, w % 2, 0:n], bank2(4, n)).then_inc(sem(n_ + "pT"), 1)
                    act.wait_ge(sem(n_ + "pv"), w + 1)
                    r = 64 * (h % 2)
                    act.copy(oT[r:r + 64, (g * GH + h) // 2, qb * P:(qb + 1) * P], ps[r:r + 64, 6 + w % 2, 0:P])\
                       .then_inc(sem(n_ + "o"), 1)

                for w in range(len(items)):
                    exps(w)
                    if w:
                        copies(w - 1)
                copies(len(items) - 1)

    def expert_scores(l, ring, pqT):
        n = f"pq{l}_"
        with nc.Block() as block:
            @block.sync
            def _(sp):
                read = {J_PQ[l] + c: (sem(n + "mm"), 4 * (c + 1)) for c in range(4)}
                load_chunk(sp, ring, J_PQ[l] + 3, read)

            @block.tensor
            def _(pe):
                for i in range(HC):
                    j = J_PQ[l] + i // 4
                    if i % 4 == 0:
                        chunk_in(pe, j)
                    if i >= 4:
                        pe.wait_ge(sem(n + "a"), i - 3)
                    w = ring[:, j % SLOTS, :].rearrange("p (c n) -> p c n", c=DC)
                    for dc in range(DC):
                        mm = product(pe, bank2(2 * (i % 4)), w[:, dc, (i % 4) * P:(i % 4 + 1) * P], hT[:, dc, :],
                                     dc == 0, dc == DC - 1)
                    mm.then_inc(sem(n + "mm"), 1)

            @block.scalar
            def _(act):
                for i in range(HC):
                    act.wait_ge(sem(n + "mm"), i + 1)
                    act.copy(pqT[:, i, :], bank2(2 * (i % 4))).then_inc(sem(n + "a"), 1)

    def expert_choice(l, pqT, keysT, selT, sc, s2, cand, c2, top, eq, pos):
        n_ = f"ch{l}_"
        vals = top[:, 0]
        idxu = pos[:, 0]
        idxf = top[:, 1]
        fs = top[:, 2, 0:HP]
        posu = pos[:, 1, 0:HP]
        pi, pj = top[:, 3, 0:HP], top[:, 3, HP:HC]
        sel = top[:, 4:6, 0:HP]
        PER = 5 * HC + 2 + 5 * HP + 2 + 2 + 1 + 6 + 3 + 1
        with nc.Block() as block:
            @block.sync
            def _(sp):
                sp.dma_start(keysT[:], inp["keysT"][l]).then_inc(sem("keys_in"), 16)

            @block.tensor
            def _(pe):
                pe.wait_ge(sem("keys_in"), 16 * (l + 1))
                for tb in range(TB):
                    if tb:
                        pe.wait_ge(sem(n_ + "sc"), tb)
                    for i in range(HC):
                        mm = pe.matmul(ps[:, i // 4, (i % 4) * P:(i % 4 + 1) * P], pqT[:, i, tb * P:(tb + 1) * P],
                                       keysT[:, i, :], start=True, stop=True)
                    mm.then_inc(sem(n_ + "s"), 1)
                    pe.wait_ge(sem(n_ + "v"), PER * (tb + 1))
                    for k in range(3):
                        src = (sel[:, 0], sel[:, 1], fs)[k].rearrange("p h k -> p (h k)")
                        mm = pe.transpose(ps[:, 4, k * P:(k + 1) * P], src, ident)
                    mm.then_inc(sem(n_ + "t"), 1)

            @block.scalar
            def _(act):
                with act.Fori(0, TB) as tb:
                    act.wait_ge(sem(n_ + "s"), tb + 1)
                    act.wait_ge(sem(n_ + "free"), tb)
                    act.copy(sc[:].rearrange("p h n -> p (h n)"), ps[:, 0:4, :].rearrange("p a n -> p (a n)"))\
                       .then_inc(sem(n_ + "sc"), 1)
                    act.wait_ge(sem(n_ + "v"), tb * PER + (5 * HC + 2 + 5 * HP + 2))
                    act.activation(fs, fs, ACT.Exp).then_inc(sem(n_ + "exp"), 1)

            @block.vector
            def _(v):
                s = sem(n_ + "v")
                with v.Fori(0, TB) as tb:
                    k = 0

                    def done(k):
                        v.wait_ge(s, tb * PER + k)
                        v.memset(small[:, 61:62], 0.0)

                    v.wait_ge(sem(n_ + "sc"), tb + 1)
                    v.memset(small[:, 61:62], 0.0)
                    for i in range(HC):
                        v.max(vals[:, i, 0:8], sc[:, i, :]).then_inc(s, 1)
                    k += HC
                    done(k)
                    for i in range(HC):
                        v.match_replace(s2[:, i, :], vals[:, i, 0:8], sc[:, i, :], NEG).then_inc(s, 1)
                    k += HC
                    done(k)
                    for i in range(HC):
                        v.max(vals[:, i, 8:16], s2[:, i, :]).then_inc(s, 1)
                        v.max_index(idxu[:, i, 0:8], vals[:, i, 0:8], sc[:, i, :]).then_inc(s, 1)
                    k += 2 * HC
                    done(k)
                    for i in range(HC):
                        v.max_index(idxu[:, i, 8:16], vals[:, i, 8:16], s2[:, i, :]).then_inc(s, 1)
                    k += HC
                    done(k)
                    v.tensor_copy(idxf, idxu).then_inc(s, 1)
                    va = vals[:, 0:HC:2, :].unsqueeze(3).to_broadcast([P, HP, 16, 16])
                    vb = vals[:, 1:HC:2, :].unsqueeze(2).to_broadcast([P, HP, 16, 16])
                    v.tensor_tensor(cand[:], va, vb, ALU.add).then_inc(s, 1)
                    k += 2
                    done(k)
                    flat = [t[:, h].rearrange("p i j -> p (i j)") for t in (cand, c2) for h in range(HP)]
                    for h in range(HP):
                        v.max(fs[:, h, 0:8], flat[h]).then_inc(s, 1)
                    k += HP
                    done(k)
                    for h in range(HP):
                        v.match_replace(flat[HP + h], fs[:, h, 0:8], flat[h], NEG).then_inc(s, 1)
                    k += HP
                    done(k)
                    for h in range(HP):
                        v.max(fs[:, h, 8:16], flat[HP + h]).then_inc(s, 1)
                        v.max_index(posu[:, h, 0:8], fs[:, h, 0:8], flat[h]).then_inc(s, 1)
                    k += 2 * HP
                    done(k)
                    for h in range(HP):
                        v.max_index(posu[:, h, 8:16], fs[:, h, 8:16], flat[HP + h]).then_inc(s, 1)
                    k += HP
                    done(k)
                    v.tensor_copy(small[:, 0:HP], fs[:, :, 0]).then_inc(s, 1)
                    k += 1
                    done(k)
                    v.tensor_tensor(fs, fs, small[:, 0:HP].unsqueeze(2).to_broadcast([P, HP, 16]), ALU.subtract)\
                     .then_inc(s, 1)
                    k += 1
                    v.tensor_scalar(pos[:, 0, 0:HP], posu, 4, None, ALU.logical_shift_right).then_inc(s, 1)
                    v.tensor_scalar(pos[:, 0, HP:HC], posu, 15, None, ALU.bitwise_and).then_inc(s, 1)
                    k += 2
                    done(k)
                    v.tensor_copy(top[:, 3], pos[:, 0]).then_inc(s, 1)
                    k += 1
                    done(k)
                    for half, rank in ((0, pi), (1, pj)):
                        if half:
                            done(k)
                        v.tensor_tensor(eq[:], rank.unsqueeze(3).to_broadcast([P, HP, 16, 16]),
                                        iota[:, 0:16].unsqueeze(1).unsqueeze(1).to_broadcast([P, HP, 16, 16]),
                                        ALU.is_equal).then_inc(s, 1)
                        k += 1
                        done(k)
                        v.tensor_tensor(eq[:], eq[:], idxf[:, half:HC:2, :].unsqueeze(2).to_broadcast([P, HP, 16, 16]),
                                        ALU.mult).then_inc(s, 1)
                        k += 1
                        done(k)
                        v.tensor_reduce(sel[:, half], eq[:], AX, ALU.add).then_inc(s, 1)
                        k += 1
                    v.wait_ge(sem(n_ + "exp"), tb + 1)
                    v.tensor_reduce(small[:, HP:2 * HP], fs, AX, ALU.add).then_inc(s, 1)
                    k += 1
                    done(k)
                    v.reciprocal(small[:, 2 * HP:3 * HP], small[:, HP:2 * HP]).then_inc(s, 1)
                    k += 1
                    done(k)
                    v.tensor_tensor(fs, fs, small[:, 2 * HP:3 * HP].unsqueeze(2).to_broadcast([P, HP, 16]), ALU.mult)\
                     .then_inc(s, 1)
                    k += 1
                    assert k == PER - 1, (k, PER)
                    done(k)
                    v.tensor_copy(small[:, 60:61], small[:, 0:1]).then_inc(s, 1)
                    v.wait_ge(sem(n_ + "t"), tb + 1)
                    v.tensor_copy(selT[:, :, bass.ds(tb * P, P)], ps[:, 4, 0:3 * P].rearrange("p (k t) -> p k t", k=3))\
                     .then_inc(sem(n_ + "free"), 1)
                    v.wait_ge(sem(n_ + "free"), tb + 1)

    def gate_matrix(l, selT, now, one1, one2, stage):
        n_ = f"gm{l}_"
        SUB = 16
        with nc.Block() as block:
            @block.vector
            def _(v):
                with v.Fori(0, T // (2 * BT)) as i:
                    for q in range(4):
                        if q < 2:
                            v.wait_ge(sem(n_ + "mm"), i * 4)
                        else:
                            v.wait_ge(sem(n_ + "mm"), i * 4 + (q - 1))
                        v.tensor_copy(now[:, q % 2], selT[:, :, bass.ds(i * (2 * BT) + q * SUB, SUB)])\
                         .then_inc(sem(n_ + "now"), 1)
                        v.wait_ge(sem(n_ + "now"), i * 4 + (q + 1))
                        for t in range(SUB):
                            v.tensor_scalar(one1[:, q % 2, t, :], iota[:], now[:, q % 2, 0, t:t + 1], None,
                                            ALU.is_equal).then_inc(sem(n_ + "one1"), 1)
                            v.tensor_scalar(one2[:, q % 2, t, :], iota[:], now[:, q % 2, 1, t:t + 1],
                                            now[:, q % 2, 2, t:t + 1], ALU.is_equal, ALU.mult)\
                             .then_inc(sem(n_ + "one2"), 1)

            @block.tensor
            def _(pe):
                with pe.Fori(0, T // (2 * BT)) as i:
                    for q in range(4):
                        b = 4 * (q % 2)
                        pe.wait_ge(sem(n_ + "one1"), i * (4 * SUB) + (q + 1) * SUB)
                        pe.wait_ge(sem(n_ + "one2"), i * (4 * SUB) + (q + 1) * SUB)
                        if q < 2:
                            pe.wait_ge(sem(n_ + "g"), i * 4)
                        else:
                            pe.wait_ge(sem(n_ + "g"), i * 4 + (q - 1))
                        for t in range(SUB):
                            mm = pe.matmul(ps[:, b + t // 4, (t % 4) * P:(t % 4 + 1) * P], one1[:, q % 2, t, :],
                                           one2[:, q % 2, t, :], start=True, stop=True)
                        mm.then_inc(sem(n_ + "mm"), 1)

            @block.scalar
            def _(act):
                with act.Fori(0, T // (2 * BT)) as i:
                    for q in range(4):
                        b = 4 * (q % 2)
                        act.wait_ge(sem(n_ + "mm"), i * 4 + (q + 1))
                        if q % 2 == 0:
                            act.wait_ge(sem(n_ + "out"), i * 32 + 16 * 0 if q == 0 else i * 32 + 0)
                        src = ps[:, b:b + 4, :].rearrange("p b (t n) -> p (b t) n", t=4)\
                            .rearrange("p t (g k) -> p t g k", k=NG)
                        dst = stage[:, q // 2, :, (q % 2) * SUB:(q % 2 + 1) * SUB, :].rearrange("p g t k -> p t g k")
                        act.copy(dst, src).then_inc(sem(n_ + "g"), 1)

            @block.sync
            def _(sp):
                with sp.Fori(0, T // (2 * BT)) as i:
                    for q in range(2):
                        sp.wait_ge(sem(n_ + "g"), i * 4 + 2 * (q + 1))
                        dst = g_dram[:, :, bass.ds(i * (2 * BT) + q * BT, BT), :].rearrange("g p t k -> p g (t k)")
                        sp.dma_start(dst, stage[:, q].rearrange("p g t k -> p g (t k)")).then_inc(sem(n_ + "out"), 16)
                sp.wait_ge(sem(n_ + "out"), 16 * (T // BT))

    def experts(l, U, Vx, G, W, Y):
        n_ = f"ex{l}_"
        HT = T // 2

        def halves(b):
            return ps[:, b:b + 2, 0:HT]

        def loads(sp, g, s, first):
            if not first:
                sp.wait_ge(sem(n_ + "a"), g * NG + (1 - 2) * NG)
            src = inp["u"][l, bass.ds(g, 1)].rearrange("a p k -> p (a k)")
            sp.dma_start(U[s].rearrange("p k c n -> p (k c n)"), src).then_inc(sem(f"u_in{s}"), 16)
            if not first:
                sp.wait_ge(sem(n_ + "w"), g * NG + (1 - 2) * NG)
            src = g_dram[bass.ds(g, 1)].rearrange("a p t k -> p (a t k)")
            sp.dma_start(G[s][:].rearrange("p t k -> p (t k)"), src).then_inc(sem(f"g_in{s}"), 16)
            if not first:
                sp.wait_ge(sem(n_ + "y"), g * DC + (1 - 2) * DC)
            src = inp["v"][l, :, bass.ds(g, 1)].rearrange("p a k -> p (a k)")
            sp.dma_start(Vx[s].rearrange("p k d -> p (k d)"), src).then_inc(sem(f"v_in{s}"), 16)

        base = 16 * (GROUPS // 2) * l
        with nc.Block() as block:
            @block.sync
            def _(sp):
                loads(sp, 0, 0, True)
                loads(sp, 1, 1, True)
                with sp.Fori(1, GROUPS // 2) as i:
                    loads(sp, i * 2, 0, False)
                    loads(sp, i * 2 + 1, 1, False)

            @block.tensor
            def _(pe):
                def up(i, s, first=False):
                    pe.wait_ge(sem(f"u_in{s}"), (i + 1) * 16 + base)
                    for k in range(NG):
                        if not (first and k < 2):
                            pe.wait_ge(sem(n_ + "gelu"), i * (2 * NG) + (NG * s + k - 1))
                        for dc in range(DC):
                            for hf in range(2):
                                mm = pe.matmul(halves(2 * (k % 2))[:, hf], U[s][:, k, dc, :],
                                               hT[:, dc, hf * HT:(hf + 1) * HT], start=dc == 0, stop=dc == DC - 1)
                        mm.then_inc(sem(n_ + "a"), 1)

                def down(i, s, first=False):
                    pe.wait_ge(sem(f"v_in{s}"), (i + 1) * 16 + base)
                    pe.wait_ge(sem(n_ + "w"), i * (2 * NG) + NG * (s + 1))
                    for db in range(DC):
                        if not (first and db < 2):
                            pe.wait_ge(sem(n_ + "yv"), i * (2 * DC) + (DC * s + db - 1))
                        for k in range(NG):
                            for hf in range(2):
                                mm = pe.matmul(halves(4 + 2 * (db % 2))[:, hf], Vx[s][:, k, db * P:(db + 1) * P],
                                               W[s][:, k, hf * HT:(hf + 1) * HT], start=k == 0, stop=k == NG - 1)
                        mm.then_inc(sem(n_ + "y"), 1)

                def down_odd(pe, i):
                    pe.wait_ge(sem("v_in1"), i * 16 + base)
                    pe.wait_ge(sem(n_ + "w"), i * (2 * NG))
                    for db in range(DC):
                        pe.wait_ge(sem(n_ + "yv"), i * (2 * DC) + (db - 1 - DC))
                        for k in range(NG):
                            for hf in range(2):
                                mm = pe.matmul(halves(4 + 2 * (db % 2))[:, hf], Vx[1][:, k, db * P:(db + 1) * P],
                                               W[1][:, k, hf * HT:(hf + 1) * HT], start=k == 0, stop=k == NG - 1)
                        mm.then_inc(sem(n_ + "y"), 1)

                up(0, 0, True)
                up(0, 1)
                down(0, 0, True)
                with pe.Fori(1, GROUPS // 2) as i:
                    up(i, 0)
                    down_odd(pe, i)
                    up(i, 1)
                    down(i, 0)
                down(GROUPS // 2 - 1, 1)

            @block.scalar
            def _(act):
                def gelus(i, s, first):
                    if not first:
                        act.wait_ge(sem(n_ + "y"), i * (2 * DC) + DC * (s - 1))
                    for k in range(NG):
                        act.wait_ge(sem(n_ + "a"), i * (2 * NG) + (NG * s + k + 1))
                        act.activation(W[s][:, k, :].rearrange("p (a n) -> p a n", a=2), halves(2 * (k % 2)),
                                       ACT.Gelu_apprx_tanh).then_inc(sem(n_ + "gelu"), 1)

                gelus(0, 0, True)
                gelus(0, 1, True)
                with act.Fori(1, GROUPS // 2) as i:
                    gelus(i, 0, False)
                    gelus(i, 1, False)

            @block.vector
            def _(v):
                v.memset(Y[:], 0.0).then_inc(sem(n_ + "y0"), 1)

                def gate(i, s):
                    v.wait_ge(sem(f"g_in{s}"), (i + 1) * 16 + base)
                    for k in range(NG):
                        v.wait_ge(sem(n_ + "gelu"), i * (2 * NG) + (NG * s + k + 1))
                        v.tensor_tensor(W[s][:, k, :], W[s][:, k, :], G[s][:, :, k], ALU.mult)\
                         .then_inc(sem(n_ + "w"), 1)

                def add(at):
                    for db in range(DC):
                        v.wait_ge(sem(n_ + "y"), at(db))
                        y = Y[:, db, :].rearrange("p (a n) -> p a n", a=2)
                        v.tensor_tensor(y, halves(4 + 2 * (db % 2)), y, ALU.add).then_inc(sem(n_ + "yv"), 1)

                v.wait_ge(sem(n_ + "y0"), 1)
                gate(0, 0)
                gate(0, 1)
                add(lambda db: db + 1)
                with v.Fori(1, GROUPS // 2) as i:
                    v.wait_ge(sem(n_ + "yv"), i * (2 * DC) - DC)
                    gate(i, 0)
                    add(lambda db: i * (2 * DC) + (db + 1 - DC))
                    v.wait_ge(sem(n_ + "yv"), i * (2 * DC))
                    gate(i, 1)
                    add(lambda db: i * (2 * DC) + (db + 1))
                v.wait_ge(sem(n_ + "yv"), (GROUPS - 1) * DC)
                add(lambda db: (GROUPS - 1) * DC + db + 1)
                v.wait_ge(sem(n_ + "yv"), GROUPS * DC)
                for dc in range(DC):
                    for c, a, b in SEG:
                        v.scalar_tensor_tensor(xT[:, dc, a:b], Y[:, dc, a:b], mod[:, l, 40 + dc, c:c + 1], xT[:, dc, a:b],
                                               ALU.mult, ALU.add).then_inc(sem(n_ + "x"), 1)

    def expert_layer(l):
        with ExitStack() as st:
            selT = sb(st, f"selT{l}", [P, 3, T])
            with ExitStack() as s2:
                pqT = sb(s2, f"pqT{l}", [P, HC, T])
                norm(l, 1, pqT)
                expert_scores(l, ring, pqT)
                with ExitStack() as s3:
                    expert_choice(l, pqT, sb(s3, f"keysT{l}", [P, HC, NK]), selT, sb(s3, f"sc{l}", [P, HC, NK]),
                                  sb(s3, f"s2{l}", [P, HC, NK]), sb(s3, f"cand{l}", [P, HP, 16, 16]),
                                  sb(s3, f"c2{l}", [P, HP, 16, 16]), sb(s3, f"top{l}", [P, 6, HC, 16]),
                                  sb(s3, f"eq{l}", [P, HP, 16, 16]), sb(s3, f"pos{l}", [P, 2, HC, 16], U32))
            with ExitStack() as s2:
                gate_matrix(l, selT, sb(s2, f"now{l}", [P, 2, 3, 16]), sb(s2, f"one1{l}", [P, 2, 16, P]),
                            sb(s2, f"one2{l}", [P, 2, 16, P]), sb(s2, f"stage{l}", [P, 2, GROUPS, BT, NG]))
        with ExitStack() as st:
            U = [ring[:, s, :].rearrange("p (k c n) -> p k c n", k=NG, c=DC) for s in range(2)]
            experts(l, U, [ring[:, 2, :].rearrange("p (k d) -> p k d", k=NG), sb(st, f"Vx{l}", [P, NG, D])[:]],
                    [sb(st, f"G{l}{s}", [P, T, NG]) for s in range(2)],
                    [sb(st, f"W{l}{s}", [P, NG, T]) for s in range(2)], sb(st, f"Y{l}", [P, DC, T]))

    with es:
        with ExitStack() as st:
            modulation(ring)
            kT = sb(st, "kT", [P, HDA, TK])
            norm(0, 0, kT[:, :, 0:T])
            qT = sb(st, "qT", [P, HDA, T])
            V = sb(st, "V", [P, 6, HDA * VDA])
            with ExitStack() as s2:
                cos, sin = sb(s2, "cos_da", [P, T]), sb(s2, "sin_da", [P, T])
                diff_qkv(ring, qT, kT, V, cos, sin, sb(s2, "scr_da", [P, 6, T]))
            with ExitStack() as s2:
                diff_attention(qT, kT, V, hT, sb(s2, "pr_da", [P, 2, 2, T]), sb(s2, "pT_da", [P, 2, T]))
            diff_subnorm(hT, kT[:, 0:4, 0:T])
            out_product(0, ring, hT, J_WO0, range(J_PQ[0], J_PQ[0] + 3))
        expert_layer(0)
        with ExitStack() as st:
            with nc.Block() as block:
                @block.sync
                def _(sp):
                    for j in range(J_WDQ, J_WDQ + 2):
                        load_chunk(sp, ring, j, {})
            with ExitStack() as s2:
                norm(1, 0, sb(s2, "sq1", [P, DC, T]))
            cqT = sb(st, "cqT", [P, 4, T])
            ckvT = sb(st, "ckvT", [P, 2, TK])
            kpeT = sb(st, "kpeT", [DR, TK])
            cos, sin = sb(st, "cos_mla", [P, TK]), sb(st, "sin_mla", [P, TK])
            with ExitStack() as s2:
                mla_compress(ring, cqT, ckvT, kpeT, cos, sin, sb(s2, "scr_c", [P, 4, T]))
            qT, kT = sb(st, "qTm", [P, GH, T]), sb(st, "kTm", [P, GH, TK])
            V = sb(st, "Vm", [P, 6, GH * DV])
            for g in range(2):
                with ExitStack() as s2:
                    mla_heads(g, ring, cqT, ckvT, kpeT, qT, kT, V, cos, sin, sb(s2, f"scr_m{g}", [16, 4, TK]),
                              sb(s2, f"xk{g}", [P, 2, TK]))
                with ExitStack() as s2:
                    mla_attention(g, qT, kT, V, hT, sb(s2, f"pr_m{g}", [P, 2, 1, T]), sb(s2, f"pT_m{g}", [P, 2, T]))
            out_product(1, ring, hT, J_WO1, range(J_PQ[1], J_PQ[1] + 3))
        expert_layer(1)
        with nc.Block() as block:
            @block.sync
            def _(sp):
                sp.dma_start(outs["y"], xT[:]).then_inc(sem("stored"), 16)
                sp.wait_ge(sem("stored"), 80)


LAM_INIT = 0.8 - 0.6 * float(np.exp(-0.3 * 0))

OUTS = {"y": (P, DC, T), "da_k": (P, HDA, TP), "da_v": (TP, HDA * VDA), "ckv": (P, 2, TP), "kpe": (DR, TP)}


def rope_tables():
    f = np.float32
    row = np.repeat(np.arange(TS // 64, dtype=f), 64)
    col = np.tile(np.arange(64, dtype=f), TS // 64)
    out = []
    for rows, width, first, d in ((64, T, 0, 64), (DQ, TK, DN, DR)):
        cos, sin = np.ones((rows, width), f), np.zeros((rows, width), f)
        h = d // 2
        inv = (f(1.0) / (f(10000.0) ** (np.arange(0, h, 2, dtype=f) / f(h)))).astype(f)
        for j in range(d):
            pos = row if j < h else col
            ang = (pos * inv[(j % h) % (h // 2)]).astype(f)
            cos[first + j, :TS], sin[first + j, :TS] = np.cos(ang), np.sin(ang)
        out.append((cos, sin))
    (c0, s0), (c1, s1) = out
    pad = lambda a: np.concatenate([a, np.zeros((P - DQ, TK), f)])
    return np.tile(c0, (2, 1)), np.tile(s0, (2, 1)), pad(c1), pad(s1)


def turn(first, d, n=P):
    m = np.zeros((n, n), np.float32)
    q = d // 4
    for j in range(d):
        a = first + j
        if (j // q) % 2 == 0:
            m[a + q, a] = -1.0
        else:
            m[a - q, a] = 1.0
    return m


def chunked(w, cols=512):
    K, N = w.shape
    a = np.asarray(w).reshape(K // P, P, N // cols, cols).transpose(2, 1, 0, 3).reshape(N // cols, P, (K // P) * cols)
    return np.pad(a, ((0, 0), (0, 0), (0, 4096 - a.shape[2])))


def kernel(**inputs):
    import concourse.bacc as bacc
    from concourse.bass_utils import run_bass_kernel_spmd

    a = {k: np.asarray(v) for k, v in inputs.items()}
    f = np.float32

    def cols(v):
        return v.reshape(-1, P).T

    wts = [chunked(a["ada_w"][l]) for l in range(2)]
    wts += [chunked(a[k][0]) for k in ("da_wq", "da_wk", "da_wv", "da_wo")]
    wts += [chunked(a["peer_wq"][0]), chunked(a["mla_wdq"][0])]
    wts += [chunked(np.pad(a["mla_wdkv"][0], ((0, 0), (0, 512 - KL - DR))))]
    for g in range(2):
        q = a["mla_wuq"][0][:, g * GH * DQ:(g + 1) * GH * DQ]
        kv = a["mla_wukv"][0][:, g * 1024:(g + 1) * 1024].reshape(KL, GH, DN + DV)
        k = np.pad(kv[:, :, :DN], ((0, 0), (0, 0), (0, DR))).reshape(2, P, GH * DQ).transpose(1, 0, 2).reshape(P, -1)
        v = kv[:, :, DN:].reshape(2, P, GH * DV).transpose(1, 0, 2).reshape(P, -1)
        kv = np.concatenate([k, v], 1)
        wts += [chunked(np.pad(q, ((0, 0), (0, 1024 - GH * DQ))), 1024),
                np.pad(kv, ((0, 0), (0, 4096 - kv.shape[1])))[None]]
    wts += [chunked(a["mla_wo"][0]), chunked(a["peer_wq"][1])]

    gains = np.zeros((P, 16), f)
    gains[:, 0], gains[:, 1] = np.tile(a["da_q_norm"][0], 2), np.tile(a["da_k_norm"][0], 2)
    gains[:, 2] = a["da_subln"][0]
    gains[:, 3:7], gains[:, 7:9] = cols(a["mla_qa_norm"][0]), cols(a["mla_kv_norm"][0])
    gains[:DQ, 9], gains[:DQ, 10] = a["mla_q_norm"][0], a["mla_k_norm"][0]
    cos0, sin0, cos1, sin1 = rope_tables()
    place = np.zeros((P, P), f)
    place[np.arange(DR), DN + np.arange(DR)] = 1.0
    ind = np.zeros((P, 3, 8, 16), f)
    indT = np.zeros((16, 2, 8, P), f)
    for h in range(8):
        for k in range(2):
            ind[64 * k:64 * k + 64, 0, h, 2 * h + k] = 1.0
            indT[2 * h + k, 0, h, 64 * k:64 * k + 64] = 1.0
        ind[:, 1, h, h] = 1.0
        ind[:DQ, 2, h, h] = 1.0
        indT[h, 1, h, :] = 1.0
    rd = turn(0, 32) + turn(32, 32)
    both = np.zeros((P, P), f)
    both[:64, :64] = turn(0, 64, 64)
    both[64:, 64:] = turn(0, 64, 64)
    del rd
    x = np.concatenate([a["x_sample"][0], a["x_prompt"][0]], 0)
    sent = {
        "xT": x.T.reshape(DC, P, T).transpose(1, 0, 2),
        "c_in": np.stack([cols(a["c"][0]), cols(a["c_ctx"])], 2),
        "norms": np.stack([cols(a["norm1"][0]), cols(a["norm1"][1]), cols(a["norm2"][0]), cols(a["norm2"][1])], 1),
        "gains": gains,
        "lam_in": np.broadcast_to(np.stack([a["da_lq1"][0], a["da_lk1"][0], a["da_lq2"][0], a["da_lk2"][0]])[None],
                                  (P, 4, DDA)),
        "ada_b": np.stack([cols(a["ada_b"][0]), cols(a["ada_b"][1])], 1),
        "consts": np.stack([np.ones((P, P), f), np.eye(P, dtype=f), both, turn(DN, DR), place], 1),
        "ind": ind,
        "indT": indT,
        "iota": np.broadcast_to(np.arange(P, dtype=f)[None], (P, P)),
        "cos_da": cos0, "sin_da": sin0, "cos_mla": cos1, "sin_mla": sin1,
        "cache_k": a["cache_da_k"][0, 0].reshape(TC, HDA, P).transpose(2, 1, 0),
        "cache_v": a["cache_da_v"][0, 0].reshape(TC, HDA * VDA),
        "cache_ckv": a["cache_mla_ckv"][0, 0].T.reshape(2, P, TC).transpose(1, 0, 2),
        "cache_kpe": a["cache_mla_kpe"][0, 0].T,
        "keysT": a["peer_keys"].reshape(2, HC, NK, P).transpose(0, 3, 1, 2),
        "u": a["peer_u"].reshape(2, NK, GROUPS, NG, DC, P).transpose(0, 2, 5, 3, 4, 1).reshape(2, GROUPS, P, NG * DC * P),
        "v": a["peer_v"].reshape(2, NK, GROUPS, NG * D),
        "wts": np.concatenate(wts, 0),
    }
    assert sent["wts"].shape[0] == N_CHUNKS
    nc = bacc.Bacc("TRN2", target_bir_lowering=False, num_devices=1)
    arrays = {"in_" + k: np.ascontiguousarray(v) for k, v in sent.items()}
    inp = {k: nc.dram_tensor("in_" + k, arrays["in_" + k].shape, F32, kind="ExternalInput").ap() for k in sent}
    outs = {k: nc.dram_tensor("out_" + k, s, F32, kind="ExternalOutput").ap() for k, s in OUTS.items()}
    g_dram = nc.dram_tensor("gates", (GROUPS, P, T, NG), F32, kind="Internal").ap()
    mixed(nc, None, inp, outs, g_dram)
    r = run_bass_kernel_spmd(nc, [arrays], core_ids=[0]).results[0]
    y = r["out_y"].transpose(1, 0, 2).reshape(D, T).T
    return (y[TS:].reshape(1, TP, D), y[:TS].reshape(1, TS, D),
            r["out_da_k"].transpose(2, 1, 0).reshape(1, 1, TP, 2 * HDA, DDA),
            r["out_da_v"].reshape(1, 1, TP, HDA, VDA),
            r["out_ckv"].transpose(2, 1, 0).reshape(1, 1, TP, KL),
            r["out_kpe"].T.reshape(1, 1, TP, DR))
```
